# Optimizing a Trainium2 kernel written in Bass

```python
import math
import jax, jax.numpy as jnp
from jax import lax
import numpy as np

D_MODEL = 2048
BATCH = 1
SEQ = 256
DEPTH = 1

EPS = 1e-6
BLOCK_Q = 128
CONV_WIDTH = D_MODEL // 2
CONV_GROUPS = 8
CONV_TAPS = 3
FOX_HEAD_DIM = 128
FOX_HEADS = (D_MODEL // 2) // FOX_HEAD_DIM
FOX_WIDTH = FOX_HEADS * FOX_HEAD_DIM
MEM_TOKENS = 256
MEM_HEADS = 4
MEM_HEAD_DIM = (D_MODEL // 2) // MEM_HEADS
MEM_WIDTH = MEM_HEADS * MEM_HEAD_DIM
N_BRANCHES = 3
D_FF = 4 * D_MODEL
IN_COLS = 3 * CONV_WIDTH + 3 * FOX_WIDTH + FOX_HEADS + MEM_WIDTH + N_BRANCHES * D_MODEL

kernel_name = "hybrid_gated_conv_fox_memxattn_block"

def _rms(x, g):
    xf = x.astype(jnp.float32)
    y = xf * lax.rsqrt(jnp.mean(xf * xf, axis=-1, keepdims=True) + EPS)
    return (y * g.astype(jnp.float32)).astype(x.dtype)

def _causal_dwconv(u, w):
    s = u.shape[1]
    up = jnp.pad(u, ((0, 0), (CONV_TAPS - 1, 0), (0, 0)))
    y = w[0] * up[:, 0:s]
    for i in range(1, CONV_TAPS):
        y = y + w[i] * up[:, i:i + s]
    return y

def _forgetting_attention(q, k, v, log_f):
    b, s, h, d = q.shape
    nb = s // BLOCK_Q
    c = jnp.cumsum(log_f, axis=1).transpose(0, 2, 1)
    qh = q.transpose(0, 2, 1, 3)
    kh = k.transpose(0, 2, 1, 3)
    vh = v.transpose(0, 2, 1, 3)
    q_blocks = qh.reshape(b, h, nb, BLOCK_Q, d).transpose(2, 0, 1, 3, 4)
    c_blocks = c.reshape(b, h, nb, BLOCK_Q).transpose(2, 0, 1, 3)
    pos_blocks = jnp.arange(s).reshape(nb, BLOCK_Q)
    kpos = jnp.arange(s)
    scale = 1.0 / math.sqrt(d)

    def one_block(args):
        qb, cb, pb = args
        logits = jnp.einsum('bhqd,bhkd->bhqk', qb, kh,
                            preferred_element_type=jnp.float32) * scale
        logits = logits + (cb[..., None] - c[:, :, None, :])
        logits = jnp.where(pb[:, None] >= kpos[None, :], logits, -jnp.inf)
        p = jax.nn.softmax(logits, axis=-1)
        return jnp.einsum('bhqk,bhkd->bhqd', p.astype(vh.dtype), vh)

    out = lax.map(one_block, (q_blocks, c_blocks, pos_blocks))
    return out.transpose(1, 0, 3, 2, 4).reshape(b, s, h * d)

def _memory_attention(qm, mem, mem_norm_g, w_mem_kv, mem_q_g, mem_k_g):
    b, s, _, _ = qm.shape
    m = mem.shape[1]
    kv = _rms(mem, mem_norm_g) @ w_mem_kv
    km = kv[..., :MEM_WIDTH].reshape(b, m, MEM_HEADS, MEM_HEAD_DIM)
    vm = kv[..., MEM_WIDTH:].reshape(b, m, MEM_HEADS, MEM_HEAD_DIM)
    qm = _rms(qm, mem_q_g)
    km = _rms(km, mem_k_g)
    logits = jnp.einsum('bshd,bmhd->bhsm', qm, km,
                        preferred_element_type=jnp.float32) / math.sqrt(MEM_HEAD_DIM)
    p = jax.nn.softmax(logits, axis=-1)
    out = jnp.einsum('bhsm,bmhd->bshd', p.astype(vm.dtype), vm)
    return out.reshape(b, s, MEM_WIDTH)

def setup_inputs(seed: int = 0) -> dict:
    key = jax.random.key(seed)
    ks = jax.random.split(key, 20)
    f32 = jnp.float32

    def nrm(k, shape, fan_in):
        return jax.random.normal(k, shape, f32) * (fan_in ** -0.5)

    def gain(k, n):
        return 1.0 + 0.02 * jax.random.normal(k, (n,), f32)

    return {
        "x": jax.random.normal(ks[0], (BATCH, SEQ, D_MODEL), f32),
        "mem": jax.random.normal(ks[1], (BATCH, MEM_TOKENS, D_MODEL), f32),
        "norm1_g": gain(ks[2], D_MODEL),
        "w_in": nrm(ks[3], (D_MODEL, IN_COLS), D_MODEL),
        "b_f": jax.random.uniform(ks[4], (FOX_HEADS,), f32, minval=1.0, maxval=4.0),
        "conv_w": nrm(ks[5], (CONV_TAPS, CONV_WIDTH), CONV_TAPS),
        "fox_q_g": gain(ks[6], FOX_HEAD_DIM),
        "fox_k_g": gain(ks[7], FOX_HEAD_DIM),
        "mem_norm_g": gain(ks[8], D_MODEL),
        "w_mem_kv": nrm(ks[9], (D_MODEL, 2 * MEM_WIDTH), D_MODEL),
        "mem_q_g": gain(ks[10], MEM_HEAD_DIM),
        "mem_k_g": gain(ks[11], MEM_HEAD_DIM),
        "w_conv_out": nrm(ks[12], (CONV_WIDTH, D_MODEL), CONV_WIDTH),
        "w_fox_out": nrm(ks[13], (FOX_WIDTH, D_MODEL), FOX_WIDTH),
        "w_mem_out": nrm(ks[14], (MEM_WIDTH, D_MODEL), MEM_WIDTH),
        "w_out": nrm(ks[15], (D_MODEL, D_MODEL), D_MODEL),
        "norm2_g": gain(ks[16], D_MODEL),
        "w_up": nrm(ks[17], (D_MODEL, D_FF), D_MODEL),
        "w_down": nrm(ks[18], (D_FF, D_MODEL), D_FF),
    }

def reference(x, mem, norm1_g, w_in, b_f, conv_w, fox_q_g, fox_k_g, mem_norm_g,
              w_mem_kv, mem_q_g, mem_k_g, w_conv_out, w_fox_out, w_mem_out,
              w_out, norm2_g, w_up, w_down):
    b, s, _ = x.shape
    for _layer in range(DEPTH):
        h = _rms(x, norm1_g)
        proj = h @ w_in
        o = 0
        conv_bg = proj[..., o:o + CONV_WIDTH]; o += CONV_WIDTH
        conv_cg = proj[..., o:o + CONV_WIDTH]; o += CONV_WIDTH
        conv_v = proj[..., o:o + CONV_WIDTH]; o += CONV_WIDTH
        fq = proj[..., o:o + FOX_WIDTH]; o += FOX_WIDTH
        fk = proj[..., o:o + FOX_WIDTH]; o += FOX_WIDTH
        fv = proj[..., o:o + FOX_WIDTH]; o += FOX_WIDTH
        f_logit = proj[..., o:o + FOX_HEADS]; o += FOX_HEADS
        mq = proj[..., o:o + MEM_WIDTH]; o += MEM_WIDTH
        gate_logit = proj[..., o:o + N_BRANCHES * D_MODEL]

        y_conv = conv_bg * _causal_dwconv(conv_cg * conv_v, conv_w)
        o_conv = y_conv @ w_conv_out

        fq = _rms(fq.reshape(b, s, FOX_HEADS, FOX_HEAD_DIM), fox_q_g)
        fk = _rms(fk.reshape(b, s, FOX_HEADS, FOX_HEAD_DIM), fox_k_g)
        fv = fv.reshape(b, s, FOX_HEADS, FOX_HEAD_DIM)
        log_f = jax.nn.log_sigmoid(f_logit.astype(jnp.float32) + b_f.astype(jnp.float32))
        o_fox = _forgetting_attention(fq, fk, fv, log_f) @ w_fox_out

        mq = mq.reshape(b, s, MEM_HEADS, MEM_HEAD_DIM)
        o_mem = _memory_attention(mq, mem, mem_norm_g, w_mem_kv, mem_q_g, mem_k_g) @ w_mem_out

        g = jax.nn.sigmoid(gate_logit).reshape(b, s, N_BRANCHES, D_MODEL)
        merged = g[:, :, 0] * o_conv + g[:, :, 1] * o_fox + g[:, :, 2] * o_mem
        x = x + merged @ w_out

        h2 = _rms(x, norm2_g)
        x = x + jnp.square(jax.nn.relu(h2 @ w_up)) @ w_down
    return x


_drawn_inputs = setup_inputs


def setup_inputs(seed=0):
    import zlib

    import numpy as np

    out = dict(_drawn_inputs(seed))
    spreads = {}
    factors = {'norm1_g': 2.925,
     'fox_q_g': 27.696,
     'fox_k_g': 32.698,
     'mem_norm_g': 8.0,
     'mem_q_g': 8.0,
     'mem_k_g': 8.0,
     'norm2_g': 13.016}
    for name, (base, spread) in spreads.items():
        noise = np.random.default_rng([zlib.crc32(name.encode()), seed]).standard_normal(out[name].shape)
        drawn = base * np.exp(spread * noise) if base else spread * noise
        out[name] = __import__('jax').numpy.asarray(drawn.astype(out[name].dtype))
    for name, factor in factors.items():
        out[name] = (out[name] * factor).astype(out[name].dtype)
    return out
```

```python
from contextlib import ExitStack

import concourse.bass as bass
from concourse import mybir

F32 = mybir.dt.float32
F32R = mybir.dt.float32r
BF16 = mybir.dt.bfloat16
ALU = mybir.AluOpType
ACT = mybir.ActivationFunctionType
AX_X = mybir.AxisListType.X

P = 128
D = 2048
TOK = 2
KT = D // P
CW = D // 2
EPS = 1e-6
NEG = -1e30
FH, MH = 8, 4
D_FF = 4 * D

COLS = 512
PK = 2
WARM = 32
PPB = KT // PK
HALF = PPB // 2
RING = 4

C_CONV_B, C_CONV_C, C_CONV_V = 0, CW, 2 * CW
C_FQ, C_FK, C_FV = 3 * CW, 4 * CW, 5 * CW
C_F = 6 * CW
C_MQ = C_F + FH
C_GATE = C_MQ + CW
NBC = CW // COLS
NBD = D // COLS

B_KV = 0
B_MQ = B_KV + NBD
B_FQ = B_MQ + NBC
B_FK = B_FQ + NBC
B_FV = B_FK + NBC
B_CC = B_FV + NBC
B_CV = B_CC + NBC
B_CB = B_CV + NBC
B_GATE = B_CB + NBC
B_PROJ = B_GATE + 3 * NBD
B_WO = B_PROJ + 3 * NBD
B_FF = B_WO + NBD
QUARTERS = D_FF // D
B_END = B_FF + 2 * NBD * QUARTERS


def first(b):
    if b <= B_PROJ:
        return PPB * b
    if b <= B_WO:
        return PPB * B_PROJ + HALF * (b - B_PROJ)
    return PPB * B_PROJ + HALF * (B_WO - B_PROJ) + PPB * (b - B_WO)


def end(b):
    return first(b + 1) - 1


def block_of(n):
    return max(b for b in range(B_END) if first(b) <= n)


def by_dve(b):
    if b < B_PROJ:
        return B_CV <= b < B_CB
    return b < B_FF or (b - B_FF) % (2 * NBD) >= NBD


def emptied(b):
    return sum(by_dve(c) == by_dve(b) for c in range(b + 1))


G_MK = 0
G_MQ = G_MK + MH
G_FQ = G_MQ + MH
G_FK = G_FQ + FH // 2
G_CONV = G_FK + FH // 2
G_MERGED = G_CONV + CW // P
G_X2 = G_MERGED + 2 * NBD
G_FF = G_X2 + 2 * NBD


def tr_bank(g):
    return 7 if g < G_CONV else 4 + g % 4


def mem_slot(h):
    return 64 + 8 * h


def fox_slot(h):
    return 96 + 6 * h


MK_SLOT, MQ_SLOT, FQ_SLOT, FK_SLOT = 28, 60, 76, 92
X_AT = 16
F_SLOT = first(B_MQ)
CONV_SLOT = first(B_GATE)
STRAIGHT = 4


def merged_end(j):
    return end(B_PROJ + 3 * j + 2)


def taken_at(b):
    return 17 if b == 0 else end(b) + 3


R_N1, R_NM, R_N2, R_CW = 0, KT, 2 * KT, 3 * KT
R_FQ = R_CW + 3 * (CW // P)
R_FK = R_FQ + 1
R_MQ = R_FK + 1
R_MK = R_MQ + 2
R_WF = R_MK + 2
WF_WIDE = 2 * FH
R_BF = R_WF + KT * FH
R_ALL = R_BF + FH


def head_slot(k):
    return mem_slot(k) if k < MH else fox_slot(k - MH)


def out_chunk(k):
    return FH + 2 * k if k < MH else k - MH


MEM_T_PARTS = (2, 2, 4, 4, 4)
MEM_SPANS = ((0, 256), (256, 512))
FOX_SPANS = ((0, P), (P, 3 * P))


def hi_groups(g):
    return max(0, g - G_MERGED)


class Steps:

    def __init__(self, dve, sem):
        self.dve, self.sem, self.n = dve, sem, 0

    def __call__(self, ins):
        self.n += 1
        ins.then_inc(self.sem, 1)
        self.dve.wait_ge(self.sem, self.n)


def build(nc, t, out):
    ctx = ExitStack()
    with ctx:
        def sb(name, shape, dt):
            return ctx.enter_context(nc.sbuf_tensor(name, shape, dt))

        def two_views(name_a, shape_a, dt_a, name_b, shape_b, dt_b):
            with ExitStack() as once:
                a = once.enter_context(nc.sbuf_tensor(name_a, shape_a, dt_a))
            return a, sb(name_b, shape_b, dt_b)

        def sem(name):
            return ctx.enter_context(nc.semaphore(name))

        raw = [sb(f"raw{i}", [P, PK, COLS], F32) for i in range(RING)]
        whi = [sb(f"whi{i}", [P, PK, COLS], F32R) for i in range(RING)]
        wlo = [sb(f"wlo{i}", [P, PK, COLS], F32R) for i in range(RING)]
        lhs_a = sb("lhs_a", [P, 2, KT, TOK * P], F32R)
        lhs_b = sb("lhs_b", [P, 2, KT, TOK * P], F32R)
        y_parts, conv = two_views("y_parts", [P, 2, CW // P, TOK * P], F32R,
                                  "conv", [P, 2, CW // P, TOK * P], F32)
        act_parts, pool_f = two_views("act_parts", [P, 2, KT, TOK * P], F32R,
                                      "wide", [P, 3 * D * TOK], F32)
        x_sb = sb("x_sb", [P, TOK, D], F32)
        wf_parts, stage = two_views("wf_parts", [P, WF_WIDE * KT + P], F32R,
                                    "stage", [P, TOK, COLS], F32)
        nlf_wide, junk = two_views("nlf_wide", [P, 2, TOK, 2, P], F32R,
                                   "junk", [P, TOK * COLS], F32)
        prob = sb("prob", [P, 520], F32)
        prob_t = sb("prob_t", [P, 512], F32)
        ident = sb("ident", [P, P], F32)
        ident_h = sb("ident_h", [P, P], BF16)
        upto = sb("upto", [P, 2 * P], F32R)
        mask = sb("mask", [P, P], BF16)
        col = sb("col", [P, R_ALL], F32)
        sm = sb("sm", [P, 240], F32)

        room = iter(range(sm.shape[1]))

        def small(n):
            at = [next(room) for _ in range(n)][0]
            return sm[:, at:at + n]

        q_sb = pool_f[:, 0:2048]
        k_sb = pool_f[:, 2048:4096]
        v_sb = pool_f[:, 4096:6144].rearrange("p (t n) -> p t n", t=TOK)
        mq_sb = pool_f[:, 6144:8192]
        mk_sb = pool_f[:, 8192:10240]
        mv_sb = pool_f[:, 10240:12288].rearrange("p (t n) -> p t n", t=TOK)
        raw_t = pool_f[:, 0:4096].rearrange("p (k m) -> p k m", k=KT)
        mem_sb = pool_f[:, 4096:8192].rearrange("p (t n) -> p t n", t=TOK)
        gates = pool_f[:, :].rearrange("p (t n) -> p t n", t=TOK)
        wf_raw, b_f = col[:, R_WF:R_BF], col[:, R_BF:R_ALL]
        u_pad, tap_sum, y_sb = prob[:, 0:2 + TOK * P], prob_t[:, 0:256], prob_t[:, 256:512]
        upto_f = stage[:, 1, 0:2 * P]
        f_rows = stage[:, 1, 0:TOK * P]
        f_sum = stage[:, 1, TOK * P:TOK * P + FH]

        conv_u = conv[:, 0, :, :].rearrange("p c m -> p (c m)")
        conv_b = conv[:, 1, :, :].rearrange("p c m -> p (c m)")

        r_mem, r_x, r_2 = small(2), small(2), small(2)
        ss_mem, ss_x, ss_2 = small(2), small(2), small(8)
        ss_k8, ss_q8 = small(16), small(16)
        ss_mk, ss_mq = small(8), small(8)
        ss_fq, ss_fk = small(16), small(16)
        var, root, inv, t_1 = small(16), small(16), small(16), small(16)
        z_neg, z_abs, z_exp, nlf = small(16), small(16), small(16), small(16)
        neg_max, p_sum, p_inv = small(2), small(2), small(2)
        ss_two = small(2)
        q_gain = small(3)

        bank = [ctx.enter_context(nc.psum_tensor(f"bank{i}", [P, 512], F32)) for i in range(8)]
        scores, p_bank, o_bank = bank[4], bank[5], bank[6]

        landed = [sem(f"landed{i}") for i in range(RING)]
        hi_ready, lo_ready = sem("hi_ready"), sem("lo_ready")
        piece_used = sem("piece_used")
        act_emptied, dve_emptied = sem("act_emptied"), sem("dve_emptied")
        mem_t_landed = [sem(f"mem_t_landed{i}") for i in range(len(MEM_T_PARTS))]
        x_t_landed = [sem(f"x_t_landed{i}") for i in range(KT // 4)]
        mem_landed = [sem(f"mem_landed{i}") for i in range(TOK)]
        x_landed = [sem(f"x_landed{i}") for i in range(TOK)]
        col_landed = sem("col_landed")
        op_hi, op_ready = sem("op_hi"), sem("op_ready")
        zeroed, consts = sem("zeroed"), sem("consts")
        upto_ready, nlf_upper = sem("upto_ready"), sem("nlf_upper")
        tr_made, tr_hi, tr_taken = sem("tr_made"), sem("tr_hi"), sem("tr_taken")
        squares, var_ready, root_ready = sem("squares"), sem("var_ready"), sem("root_ready")
        mem_scaled, x_scaled = sem("mem_scaled"), sem("x_scaled")
        normed = sem("normed")
        wf_hi, wf_lo, f_made = sem("wf_hi"), sem("wf_lo"), sem("f_made")
        f_rows_ready, f_summed = sem("f_rows_ready"), sem("f_summed")
        abs_ready, exp_ready, one_more, log_ready = (sem("abs_ready"), sem("exp_ready"),
                                                     sem("one_more"), sem("log_ready"))
        nlf_ready, nlf_spread = sem("nlf_ready"), sem("nlf_spread")
        scores_made, max_ready, exp_done = sem("scores_made"), sem("max_ready"), sem("exp_done")
        p_normed, pt_made, pt_taken = sem("p_normed"), sem("pt_made"), sem("pt_taken")
        pv_made, o_hi, pv_taken = sem("pv_made"), sem("o_hi"), sem("pv_taken")
        pad_ready, y_hi, y_lo = sem("pad_ready"), sem("y_hi"), sem("y_lo")
        merged_ready, x2_ready = sem("merged_ready"), sem("x2_ready")
        norm2_ready = sem("norm2_ready")
        relu_ready, sq_ready = sem("relu_ready"), sem("sq_ready")
        dve_step = sem("dve_step")
        tail_ready, stored = sem("tail_ready"), sem("stored")

        w_in = t["w_in"].rearrange("(k p) n -> p k n", p=P)
        w_kv = t["w_mem_kv"].rearrange("(k p) n -> p k n", p=P)
        w_branch = [t[n].rearrange("(k p) n -> p k n", p=P)
                    for n in ("w_conv_out", "w_fox_out", "w_mem_out")]
        w_out = t["w_out"].rearrange("(k p) n -> p k n", p=P)
        w_up = t["w_up"].rearrange("(k p) n -> p k n", p=P)
        w_down = t["w_down"].rearrange("(q k p) n -> q p k n", p=P, k=KT)
        mem_t_dram, x_t_dram = [t[n].rearrange("p (k m) -> p k m", k=KT) for n in ("mem_t", "x_t")]
        x_dram = t["x"].rearrange("b (t p) n -> p (b t) n", p=P)
        mem_dram = t["mem"].rearrange("b (t p) n -> p (b t) n", p=P)
        out_dram = out.rearrange("b (t p) n -> p (b t) n", p=P)

        def projection_column(b):
            for at, start in ((B_GATE, C_GATE), (B_CB, C_CONV_B), (B_CV, C_CONV_V),
                              (B_CC, C_CONV_C), (B_FV, C_FV), (B_FK, C_FK), (B_FQ, C_FQ),
                              (B_MQ, C_MQ)):
                if b >= at:
                    return start + COLS * (b - at)

        def source(b):
            if b < B_MQ:
                return w_kv[:, :, COLS * b:COLS * (b + 1)]
            if b < B_PROJ:
                c = projection_column(b)
                return w_in[:, :, c:c + COLS]
            if b < B_WO:
                j, branch = divmod(b - B_PROJ, 3)
                return w_branch[branch][:, :, COLS * j:COLS * (j + 1)]
            j = b - B_WO
            return w_out[:, :, COLS * j:COLS * (j + 1)]

        block = ctx.enter_context(nc.Block())

        @block.sync
        def _(sp):
            def load(n, src, base=None):
                if base is not None:
                    sp.wait_ge(lo_ready, base + (n - RING + 1))
                elif n >= RING:
                    sp.wait_ge(lo_ready, n - RING + 1)
                sp.dma_start(raw[n % RING][:], src).then_inc(landed[n % RING], 16)

            def load_block(b):
                for k in range(0, KT if not B_PROJ <= b < B_WO else CW // P, PK):
                    load(first(b) + k // PK, source(b)[:, k:k + PK, :])

            sp.dma_start(col[:], t["cols"]).then_inc(col_landed, 16)
            for n in range(first(B_MQ)):
                if n in (0, 1, 2, 4, 5):
                    c = (0, 1, 2, 4, 5).index(n)
                    s = slice(sum(MEM_T_PARTS[:c]), sum(MEM_T_PARTS[:c + 1]))
                    sp.dma_start(raw_t[:, s, :], mem_t_dram[:, s, :]).then_inc(mem_t_landed[c], 16)
                k = PK * (n % PPB)
                load(n, source(block_of(n))[:, k:k + PK, :])
                if n in (8, 10):
                    tok = (n - 8) // 2
                    sp.dma_start(mem_sb[:, tok, :], mem_dram[:, tok, :]).then_inc(mem_landed[tok], 16)
                if n in (12, 13, 14, 15):
                    c = n - 12
                    s = slice(4 * c, 4 * (c + 1))
                    sp.dma_start(raw_t[:, s, :], x_t_dram[:, s, :]).then_inc(x_t_landed[c], 16)
                if n in (17, 19):
                    tok = (n - 17) // 2
                    sp.dma_start(x_sb[:, tok, :], x_dram[:, tok, :]).then_inc(x_landed[tok], 16)
            for b in range(B_MQ, B_GATE + STRAIGHT):
                load_block(b)
            with sp.Fori(0, (B_PROJ - B_GATE - STRAIGHT) // 2) as i:
                for n in range(2 * PPB):
                    b, k = divmod(n, PPB)
                    c = bass.ds(i * (2 * COLS) + (C_GATE + COLS * (STRAIGHT + b)), COLS)
                    load(first(B_GATE + STRAIGHT) + n, w_in[:, PK * k:PK * k + PK, c],
                         base=i * (2 * PPB))
            for b in range(B_PROJ, B_FF):
                load_block(b)
            for b in range(NBD):
                for k in range(PPB):
                    load(first(B_FF + b) + k, w_up[:, PK * k:PK * k + PK, COLS * b:COLS * (b + 1)])
            for b in range(NBD):
                for k in range(PPB):
                    load(first(B_FF + NBD + b) + k,
                         w_down[0, :, PK * k:PK * k + PK, COLS * b:COLS * (b + 1)])
            with sp.Fori(0, QUARTERS - 1) as i:
                for n in range(2 * NBD * PPB):
                    b, k = divmod(n, PPB)
                    if b < NBD:
                        src = w_up[:, PK * k:PK * k + PK, bass.ds(i * D + (D + COLS * b), COLS)]
                    else:
                        src = w_down[bass.ds(i + 1, 1), :, PK * k:PK * k + PK,
                                     COLS * (b - NBD):COLS * (b - NBD + 1)]
                        src = src.rearrange("q p k n -> (q p) k n")
                    load(first(B_FF + 2 * NBD) + n, src, base=i * (2 * NBD * PPB))
            for j in range(NBD - 1):
                sp.wait_ge(dve_emptied, emptied(B_END - NBD + j))
                sp.dma_start(out_dram[:, :, COLS * j:COLS * (j + 1)],
                             x_sb[:, :, COLS * j:COLS * (j + 1)]).then_inc(stored, 16)
            for tok in range(TOK):
                sp.wait_ge(tail_ready, tok + 1)
                sp.dma_start(out_dram[:, tok, D - COLS:D],
                             x_sb[:, tok, D - COLS:D]).then_inc(stored, 16)
            sp.wait_ge(stored, 16 * (NBD - 1 + TOK))

        @block.gpsimd
        def _(pool):
            pool.memset(ident[:], 0.0).then_inc(zeroed, 1)
            pool.memset(ident_h[:], 0.0).then_inc(zeroed, 1)
            pool.memset(upto_f, 1.0).then_inc(zeroed, 1)
            pool.memset(mask[:], 0.0).then_inc(zeroed, 1)
            pool.wait_ge(zeroed, 4)
            for m in (ident, ident_h):
                pool.affine_select(out=m[:], in_=m[:], compare_op=ALU.not_equal, fill=1.0, base=0,
                                   pattern=[[-1, P]], channel_multiplier=1).then_inc(consts, 1)
            pool.affine_select(out=upto_f[:, 0:P], in_=upto_f[:, 0:P], compare_op=ALU.is_ge, fill=0.0,
                               base=0, pattern=[[1, P]], channel_multiplier=-1).then_inc(consts, 1)
            pool.affine_select(out=mask[:], in_=mask[:], compare_op=ALU.is_ge, fill=NEG, base=0,
                               pattern=[[-1, P]], channel_multiplier=1).then_inc(consts, 1)
            pool.wait_ge(nlf_ready, 1)
            pool.wait_ge(normed, 4)
            for h in range(FH):
                if h >= 2:
                    pool.wait_ge(scores_made, MH + h - 1)
                for tok in range(TOK):
                    wide = nlf[:, FH * tok + h:FH * tok + h + 1].to_broadcast([P, P])
                    hi, lo = nlf_wide[:, h % 2, tok, 0, :], nlf_wide[:, h % 2, tok, 1, :]
                    pool.tensor_copy(hi, wide).then_inc(nlf_upper, 1)
                    pool.wait_ge(nlf_upper, TOK * h + tok + 1)
                    last = pool.tensor_tensor(lo, wide, hi.bitcast(F32), ALU.subtract)
                last.then_inc(nlf_spread, 1)

        @block.scalar
        def _(act):
            def split(n, base=0, base16=0):
                act.wait_ge(landed[n % RING], base16 + 16 * (n // RING + 1))
                if n >= RING:
                    act.wait_ge(piece_used, base + (n - RING + 1))
                act.activation(whi[n % RING][:], raw[n % RING][:], ACT.Copy).then_inc(hi_ready, 1)

            def empty(b, outs, scale, func=ACT.Copy, base=0):
                act.wait_ge(piece_used, base + (end(b) + 1))
                for tok in range(TOK):
                    src = bank[2 * (b % 2) + tok][:]
                    if len(outs[tok].shape) == 3:
                        src = src.rearrange("p (c n) -> p c n", n=P)
                    last = act.activation(outs[tok], src, func, scale=scale[:, tok:tok + 1])
                last.then_inc(act_emptied, 1)

            def by_head(region, c):
                v = region.rearrange("p (c t n) -> p c t n", t=TOK, n=P)
                return [v[:, 4 * c:4 * c + 4, tok, :] for tok in range(TOK)]

            def by_token(region, c):
                return [region[:, tok, COLS * c:COLS * (c + 1)] for tok in range(TOK)]

            def operand_hi(g, dst, k, gain):
                act.wait_ge(tr_made, g + 1)
                for j in range(PK):
                    last = act.activation(dst[:, 0, k + j, :],
                                          bank[tr_bank(g)][:, 256 * j:256 * (j + 1)], ACT.Copy,
                                          scale=col[:, gain + k + j:gain + k + j + 1])
                last.then_inc(tr_hi, 1)

            def square_root(i, n):
                act.wait_ge(var_ready, i + 1)
                act.activation(root[:, 0:n], var[:, 0:n], ACT.Sqrt).then_inc(root_ready, 1)

            def exponentials(k, spans):
                act.wait_ge(max_ready, k + 1)
                if k:
                    act.wait_ge(pt_made, k)
                for i, (a, b) in enumerate(spans):
                    act.activation(prob[:, a:b], scores[:, a:b], ACT.Exp, bias=neg_max[:, i:i + 1],
                                   accum_out=p_sum[:, i:i + 1]).then_inc(exp_done, 1)

            def attention_out_hi(k, chunk, n):
                act.wait_ge(pv_made, k + 1)
                act.activation(lhs_b[:, 0, chunk:chunk + n, :],
                               o_bank[:, 0:256 * n].rearrange("p (c n) -> p c n", c=n),
                               ACT.Copy).then_inc(o_hi, 1)

            act.wait_ge(consts, 4)
            act.activation(upto[:], upto_f, ACT.Copy).then_inc(upto_ready, 1)
            act.wait_ge(col_landed, 16)

            def operand_hi_raw(i, dst, k, gain):
                for j in range(PK):
                    last = act.activation(dst[:, 0, k + j, :], raw_t[:, k + j, :], ACT.Copy,
                                          scale=col[:, gain + k + j:gain + k + j + 1])
                last.then_inc(op_hi, 1)

            for n in range(first(B_GATE + STRAIGHT)):
                if n < PPB:
                    for c in range(len(MEM_T_PARTS)):
                        if PK * n == sum(MEM_T_PARTS[:c]):
                            act.wait_ge(mem_t_landed[c], 16)
                    operand_hi_raw(n, lhs_b, PK * n, R_NM)
                split(n)
                if n in (11, 13):
                    tok = (n - 11) // 2
                    act.wait_ge(mem_landed[tok], 16)
                    act.activation(mem_sb[:, tok, :], mem_sb[:, tok, :], ACT.Square,
                                   accum_out=ss_mem[:, tok:tok + 1]).then_inc(squares, 1)
                if n in (21, 23):
                    tok = (n - 21) // 2
                    act.wait_ge(x_landed[tok], 16)
                    act.wait_ge(squares, 2 + tok)
                    act.activation(mem_sb[:, tok, :], x_sb[:, tok, :], ACT.Square,
                                   accum_out=ss_x[:, tok:tok + 1]).then_inc(squares, 1)
                j = n - X_AT
                if j % 2 == 0 and 0 <= j // 2 < PPB:
                    if j % 4 == 0:
                        act.wait_ge(x_t_landed[j // 4], 16)
                    operand_hi_raw(PPB + j // 2, lhs_a, PK * (j // 2), R_N1)
                if n == 24:
                    v = wf_parts[:, 0:WF_WIDE * KT].rearrange("p (k a n) -> p a k n", a=2, n=FH)
                    act.activation(v[:, 0], wf_raw.rearrange("p (k n) -> p k n", n=FH),
                                   ACT.Copy).then_inc(wf_hi, 1)
                for i, (at, width) in enumerate(((15, 2), (23, 8), (31, 2), (53, 8), (69, 16), (85, 16))):
                    if n == at:
                        square_root(i, width)
                if n == F_SLOT + 7:
                    act.wait_ge(abs_ready, 1)
                    act.activation(z_exp, z_abs, ACT.Exp, scale=-1.0).then_inc(exp_ready, 1)
                if n == F_SLOT + 8:
                    act.wait_ge(one_more, 1)
                    act.activation(z_abs, z_exp, ACT.Ln).then_inc(log_ready, 1)
                for b in range(max(0, block_of(n) - 2), block_of(n) + 1):
                    if n != taken_at(b) or by_dve(b):
                        continue
                    if b == B_KV:
                        act.wait_ge(mem_scaled, 1)
                    if b == B_MQ:
                        act.wait_ge(x_scaled, 1)
                    if b < B_KV + NBC:
                        empty(b, by_head(mk_sb, b), r_mem)
                    elif b < B_MQ:
                        empty(b, by_token(mv_sb, b - NBC), r_mem)
                    elif b < B_FQ:
                        empty(b, by_head(mq_sb, b - B_MQ), r_x)
                    elif b < B_FK:
                        empty(b, by_head(q_sb, b - B_FQ), r_x)
                    elif b < B_FV:
                        empty(b, by_head(k_sb, b - B_FK), r_x)
                    elif b < B_CC:
                        empty(b, by_token(v_sb, b - B_FV), r_x)
                    elif b < B_CV:
                        empty(b, by_head(conv_u, b - B_CC), r_x)
                    elif b < B_GATE:
                        empty(b, by_head(conv_b, b - B_CB), r_x)
                    else:
                        if b == B_GATE:
                            act.wait_ge(pv_made, MH + FH)
                        empty(b, by_token(gates, b - B_GATE), r_x, ACT.Sigmoid)
                for k in range(MH + FH):
                    s = head_slot(k)
                    if n == s + 3:
                        exponentials(k, MEM_SPANS if k < MH else FOX_SPANS)
                    if n == s + 9:
                        attention_out_hi(k, out_chunk(k), 2 if k < MH else 1)
                for c in range(CW // P):
                    s = CONV_SLOT + 3 * c
                    if n == s + 3:
                        g = G_CONV + c
                        act.wait_ge(tr_made, g + 1)
                        act.wait_ge(tr_taken, g)
                        act.activation(u_pad[:, 2:2 + TOK * P], bank[tr_bank(g)][:, 0:TOK * P],
                                       ACT.Copy).then_inc(pad_ready, 1)
                    if n == s + 4:
                        act.wait_ge(tr_taken, G_CONV + c + 1)
                        act.activation(y_parts[:, 0, c, :], y_sb, ACT.Copy).then_inc(y_hi, 1)

            with act.Fori(0, (B_PROJ - B_GATE - STRAIGHT) // 2) as i:
                n0, b0 = first(B_GATE + STRAIGHT), B_GATE + STRAIGHT
                for j in range(2 * PPB):
                    split(n0 + j, base=i * (2 * PPB), base16=i * (8 * PPB))
                    if j in (2, PPB + 2):
                        b = b0 - 1 + j // PPB
                        cols = bass.ds(i * (2 * COLS) + COLS * (b - B_GATE), COLS)
                        empty(b, [gates[:, tok, cols] for tok in range(TOK)], r_x, ACT.Sigmoid,
                              base=i * (2 * PPB))

            def plain_hi(g, k, dst, base=0):
                act.wait_ge(tr_made, base + (g + 1))
                act.activation(dst[:, 0, k:k + PK, :],
                               bank[tr_bank(g)][:].rearrange("p (c n) -> p c n", c=PK),
                               ACT.Copy).then_inc(tr_hi, 1)

            def relu(b, q0, k, base=0, baseq=0):
                act.wait_ge(piece_used, base + (end(b) + 1))
                if q0 or k:
                    act.wait_ge(tr_made, baseq + (G_FF + 2 * NBD * q0 + 2 * k))
                for tok in range(TOK):
                    last = act.activation(stage[:, tok, :], bank[2 * (b % 2) + tok][:], ACT.Relu,
                                          scale=r_2[:, tok:tok + 1])
                last.then_inc(act_emptied, 1)

            for n in range(first(B_PROJ), first(B_FF + 2 * NBD)):
                split(n)
                if n == taken_at(B_PROJ - 1):
                    empty(B_PROJ - 1, by_token(gates, B_PROJ - 1 - B_GATE), r_x, ACT.Sigmoid)
                for j in range(NBD):
                    for a in range(2):
                        if n == merged_end(j) + 6 + a:
                            plain_hi(G_MERGED + 2 * j + a, 4 * j + 2 * a, lhs_a)
                    e = end(B_WO + j)
                    if n == e + 4:
                        act.wait_ge(dve_emptied, emptied(B_WO + j))
                        for tok in range(TOK):
                            if j or tok:
                                act.wait_ge(squares, 4 + 2 * j + tok)
                            act.activation(junk[:, 0:COLS], x_sb[:, tok, COLS * j:COLS * (j + 1)],
                                           ACT.Square, accum_out=ss_2[:, NBD * tok + j:NBD * tok + j + 1]
                                           ).then_inc(squares, 1)
                    for a in range(2):
                        if n == e + 6 + a:
                            operand_hi(G_X2 + 2 * j + a, lhs_b, 4 * j + 2 * a, R_N2)
                    e = end(B_FF + j)
                    if n == e + 3:
                        if j == 0:
                            act.wait_ge(norm2_ready, 1)
                        relu(B_FF + j, 0, j)
                    for a in range(2):
                        if n == e + 6 + a:
                            plain_hi(G_FF + 2 * j + a, 4 * j + 2 * a, act_parts)
                if n == end(B_WO + NBD - 1) + 5:
                    square_root(6, 2)

            with act.Fori(0, QUARTERS - 1) as i:
                n0, b0 = first(B_FF + 2 * NBD), B_FF + 2 * NBD
                by_n, by_g = i * (2 * NBD * PPB), i * (2 * NBD)
                for m in range(2 * NBD * PPB):
                    split(n0 + m, base=by_n, base16=i * (8 * NBD * PPB))
                    for k in range(NBD):
                        if m == PPB * k + 10:
                            relu(b0 + k, 1, k, base=by_n, baseq=by_g)
                        for a in range(2):
                            if m == PPB * k + 13 + a:
                                plain_hi(G_FF + 2 * NBD + 2 * k + a, 4 * k + 2 * a, act_parts,
                                          base=by_g)

        @block.vector
        def _(dve):
            step = Steps(dve, dve_step)

            def split(n, base=0):
                dve.wait_ge(hi_ready, base + (n + 1))
                dve.tensor_tensor(wlo[n % RING][:], raw[n % RING][:], whi[n % RING][:].bitcast(F32),
                                  ALU.subtract).then_inc(lo_ready, 1)

            def operand_lo(g, dst, k, gain):
                dve.wait_ge(tr_hi, hi_groups(g) + 1)
                for j in range(PK):
                    last = dve.scalar_tensor_tensor(
                        dst[:, 1, k + j, :], bank[tr_bank(g)][:, 256 * j:256 * (j + 1)],
                        col[:, gain + k + j:gain + k + j + 1],
                        dst[:, 0, k + j, :].bitcast(F32), ALU.mult, ALU.subtract)
                last.then_inc(tr_taken, 1)

            def operand_lo_raw(i, dst, k, gain):
                dve.wait_ge(op_hi, i + 1)
                for j in range(PK):
                    last = dve.scalar_tensor_tensor(dst[:, 1, k + j, :], raw_t[:, k + j, :],
                                                    col[:, gain + k + j:gain + k + j + 1],
                                                    dst[:, 0, k + j, :].bitcast(F32),
                                                    ALU.mult, ALU.subtract)
                last.then_inc(op_ready, 1)

            def plain_lo(g, k, dst, base=0):
                dve.wait_ge(tr_hi, base + (hi_groups(g) + 1))
                dve.tensor_tensor(dst[:, 1, k:k + PK, :],
                                  bank[tr_bank(g)][:].rearrange("p (c n) -> p c n", c=PK),
                                  dst[:, 0, k:k + PK, :].bitcast(F32),
                                  ALU.subtract).then_inc(tr_taken, 1)

            def variance(ss, n, width):
                step(dve.tensor_scalar(var[:, 0:n], ss, 1.0 / width, EPS, ALU.mult, ALU.add))
                dve.sem_inc(var_ready, 1)

            def inverse_root(i, n, dst, done=None):
                dve.wait_ge(root_ready, i + 1)
                a, y, u = var[:, 0:n], inv[:, 0:n], t_1[:, 0:n]
                step(dve.reciprocal(y, root[:, 0:n]))
                step(dve.tensor_tensor(u, y, y, ALU.mult))
                step(dve.tensor_tensor(u, u, a, ALU.mult))
                step(dve.tensor_scalar(u, u, -0.5, 1.5, ALU.mult, ALU.add))
                last = dve.tensor_tensor(dst, y, u, ALU.mult)
                if done is None:
                    step(last)
                else:
                    last.then_inc(done, 1)
                    dve.wait_ge(done, 1)

            def head_squares(b, region, c, dst):
                dve.wait_ge(act_emptied, emptied(b))
                part = region[:, 1024 * c:1024 * (c + 1)]
                step(dve.tensor_tensor(junk[:], part, part, ALU.mult))
                step(dve.tensor_reduce(dst, junk[:].rearrange("p (c n) -> p c n", n=P), AX_X, ALU.add))

            def scale_heads(region, r, halves):
                v = region.rearrange("p (h a t n) -> p a t h n", a=halves, t=TOK, n=P)
                r = r.rearrange("p (h t) -> p t h", t=TOK)
                for a in range(halves):
                    for tok in range(TOK):
                        w = v[:, a, tok]
                        last = dve.tensor_tensor(w, w, r[:, tok].unsqueeze(2).to_broadcast(w.shape),
                                                 ALU.mult)
                last.then_inc(normed, 1)

            def head_taken(g, region, at, gains):
                dve.wait_ge(tr_made, g + 1)
                w = 512 // len(gains)
                for j, gain in enumerate(gains):
                    last = dve.tensor_scalar(region[:, 512 * at + w * j:512 * at + w * (j + 1)],
                                             bank[tr_bank(g)][:, w * j:w * (j + 1)], gain, None,
                                             ALU.mult)
                last.then_inc(tr_taken, 1)

            for n in range(first(B_GATE + STRAIGHT)):
                if n == 0:
                    dve.wait_ge(col_landed, 16)
                    step(dve.tensor_scalar(q_gain[:, 0:1], col[:, R_FQ:R_FQ + 1], float(P) ** -0.5,
                                           None, ALU.mult))
                    step(dve.tensor_scalar(q_gain[:, 1:3], col[:, R_MQ:R_MQ + 2],
                                           float(2 * P) ** -0.5, None, ALU.mult))
                if n < PPB:
                    operand_lo_raw(n, lhs_b, PK * n, R_NM)
                split(n)
                if n == 14:
                    dve.wait_ge(squares, 2)
                    variance(ss_mem, 2, D)
                if n == 16:
                    inverse_root(0, 2, r_mem, mem_scaled)
                if n == 30:
                    dve.wait_ge(squares, 4)
                    variance(ss_x, 2, D)
                if n == 32:
                    inverse_root(2, 2, r_x, x_scaled)
                if n in (18, 21):
                    c = (n - 18) // 3
                    head_squares(c, mk_sb, c, ss_k8[:, 8 * c:8 * c + 8])
                if n in (45, 51):
                    c = (n - 45) // 6
                    head_squares(B_MQ + c, mq_sb, c, ss_q8[:, 8 * c:8 * c + 8])
                if n in (60, 67):
                    c = (n - 60) // 7
                    head_squares(B_FQ + c, q_sb, c, ss_fq[:, 8 * c:8 * c + 8])
                if n in (76, 83):
                    c = (n - 76) // 7
                    head_squares(B_FK + c, k_sb, c, ss_fk[:, 8 * c:8 * c + 8])
                if n in (22, 52):
                    ss8, ss = (ss_k8, ss_mk) if n == 22 else (ss_q8, ss_mq)
                    pair = ss8.rearrange("p (h a t) -> p a h t", a=2, t=TOK)
                    step(dve.tensor_tensor(ss.rearrange("p (h t) -> p h t", t=TOK), pair[:, 0],
                                           pair[:, 1], ALU.add))
                    variance(ss, 8, 2 * P)
                if n == 68:
                    variance(ss_fq, 16, P)
                if n == 84:
                    variance(ss_fk, 16, P)
                if n == 24:
                    inverse_root(1, 8, ss_mk)
                if n == 54:
                    inverse_root(3, 8, ss_mq)
                if n == 70:
                    inverse_root(4, 16, ss_fq)
                if n == 86:
                    inverse_root(5, 16, ss_fk)
                if n == 25:
                    scale_heads(mk_sb, ss_mk, 2)
                if n == 55:
                    scale_heads(mq_sb, ss_mq, 2)
                if n == 72:
                    scale_heads(q_sb, ss_fq, 1)
                if n == 88:
                    scale_heads(k_sb, ss_fk, 1)
                j = n - X_AT
                if j % 2 == 0 and 0 <= j // 2 < PPB:
                    operand_lo_raw(PPB + j // 2, lhs_a, PK * (j // 2), R_N1)
                for j in range(4):
                    if n == MK_SLOT + 3 + 2 * j:
                        head_taken(G_MK + j, mk_sb, j, [col[:, R_MK:R_MK + 1], col[:, R_MK + 1:R_MK + 2]])
                    if n == MQ_SLOT + 3 + j:
                        head_taken(G_MQ + j, mq_sb, j, [q_gain[:, 1:2], q_gain[:, 2:3]])
                    if n == FQ_SLOT + 3 + j:
                        head_taken(G_FQ + j, q_sb, j, [q_gain[:, 0:1]])
                    if n == FK_SLOT + 3 + j:
                        head_taken(G_FK + j, k_sb, j, [col[:, R_FK:R_FK + 1]])
                if n == 26:
                    dve.wait_ge(wf_hi, 1)
                    v = wf_parts[:, 0:WF_WIDE * KT].rearrange("p (k a n) -> p a k n", a=2, n=FH)
                    dve.memset(wf_parts[:, WF_WIDE * KT:].bitcast(F32), 0.0)
                    step(dve.tensor_tensor(f_sum[0:WF_WIDE, :], ident[0:WF_WIDE, 0:FH],
                                           ident[0:WF_WIDE, FH:2 * FH], ALU.add))
                    dve.tensor_tensor(v[:, 1], wf_raw.rearrange("p (k n) -> p k n", n=FH),
                                      v[:, 0].bitcast(F32), ALU.subtract).then_inc(wf_lo, 1)
                if n == F_SLOT + 3:
                    dve.wait_ge(f_made, 1)
                    dve.tensor_copy(f_rows[0:WF_WIDE, :],
                                    o_bank[0:WF_WIDE, 0:TOK * P]).then_inc(f_rows_ready, 1)
                if n == F_SLOT + 7:
                    dve.wait_ge(f_summed, 1)
                    for tok in range(TOK):
                        s = slice(FH * tok, FH * (tok + 1))
                        step(dve.scalar_tensor_tensor(z_exp[:, s],
                                                      o_bank[:, 256 + s.start:256 + s.stop], r_x[:, tok:tok + 1],
                                                      b_f, ALU.mult, ALU.add))
                    step(dve.tensor_scalar(z_neg, z_exp, -1.0, None, ALU.mult))
                    dve.tensor_tensor(z_abs, z_exp, z_neg, ALU.max).then_inc(abs_ready, 1)
                if n == F_SLOT + 8:
                    dve.wait_ge(exp_ready, 1)
                    dve.tensor_scalar(z_exp, z_exp, 1.0, None, ALU.add).then_inc(one_more, 1)
                if n == F_SLOT + 9:
                    dve.wait_ge(log_ready, 1)
                    dve.scalar_tensor_tensor(nlf, z_neg, 0.0, z_abs, ALU.max,
                                             ALU.add).then_inc(nlf_ready, 1)
                for b in (B_CV, B_CV + 1):
                    if n == taken_at(b):
                        dve.wait_ge(piece_used, end(b) + 1)
                        dve.wait_ge(act_emptied, emptied(B_CV - 1))
                        v = conv_u.rearrange("p (c t n) -> p c t n", t=TOK, n=P)
                        for tok in range(TOK):
                            u = v[:, 4 * (b - B_CV):4 * (b - B_CV) + 4, tok, :]
                            last = dve.scalar_tensor_tensor(
                                u, bank[2 * (b % 2) + tok][:].rearrange("p (c n) -> p c n", n=P),
                                r_x[:, tok:tok + 1], u, ALU.mult, ALU.mult)
                        last.then_inc(dve_emptied, 1)
                for k in range(MH + FH):
                    s = head_slot(k)
                    spans = MEM_SPANS if k < MH else FOX_SPANS
                    if n == s + 3:
                        dve.wait_ge(scores_made, k + 1)
                        for i, (a, b) in enumerate(spans):
                            last = dve.tensor_reduce(neg_max[:, i:i + 1], scores[:, a:b], AX_X, ALU.max,
                                                     negate=True)
                        last.then_inc(max_ready, 1)
                    if n == s + 4:
                        dve.wait_ge(exp_done, 2 * (k + 1))
                        step(dve.reciprocal(p_inv, p_sum))
                        for i, (a, b) in enumerate(spans):
                            last = dve.tensor_scalar(prob[:, a:b], prob[:, a:b], p_inv[:, i:i + 1], None,
                                                     ALU.mult)
                        last.then_inc(p_normed, 1)
                    if n == s + 7:
                        w = 512 if k < MH else 384
                        dve.wait_ge(pt_made, k + 1)
                        dve.tensor_copy(prob_t[:, 0:w], p_bank[:, 0:w]).then_inc(pt_taken, 1)
                    if n == s + 9:
                        c, m = out_chunk(k), 2 if k < MH else 1
                        dve.wait_ge(o_hi, k + 1)
                        dve.tensor_tensor(lhs_b[:, 1, c:c + m, :],
                                          o_bank[:, 0:256 * m].rearrange("p (c n) -> p c n", c=m),
                                          lhs_b[:, 0, c:c + m, :].bitcast(F32),
                                          ALU.subtract).then_inc(pv_taken, 1)
                if n == CONV_SLOT + 2:
                    step(dve.memset(u_pad[:, 0:2], 0.0))
                for c in range(CW // P):
                    s = CONV_SLOT + 3 * c
                    if n == s + 3:
                        g = G_CONV + c
                        taps = [col[:, R_CW + CW // P * a + c:R_CW + CW // P * a + c + 1]
                                for a in range(3)]
                        dve.wait_ge(pad_ready, c + 1)
                        step(dve.tensor_scalar(tap_sum, u_pad[:, 0:TOK * P], taps[0], None, ALU.mult))
                        for a in (1, 2):
                            step(dve.scalar_tensor_tensor(tap_sum, u_pad[:, a:a + TOK * P], taps[a],
                                                          tap_sum, ALU.mult, ALU.add))
                        dve.tensor_tensor(y_sb, tap_sum, bank[tr_bank(g)][:, 256:512],
                                          ALU.mult).then_inc(tr_taken, 1)
                    if n == s + 4:
                        dve.wait_ge(y_hi, c + 1)
                        dve.tensor_tensor(y_parts[:, 1, c, :], y_sb, y_parts[:, 0, c, :].bitcast(F32),
                                          ALU.subtract).then_inc(y_lo, 1)
                        dve.wait_ge(y_lo, c + 1)

            with dve.Fori(0, (B_PROJ - B_GATE - STRAIGHT) // 2) as i:
                for j in range(2 * PPB):
                    split(first(B_GATE + STRAIGHT) + j, base=i * (2 * PPB))

            def add_to_x(b, j, base=0, basee=0):
                dve.wait_ge(piece_used, base + (end(b) + 1))
                dve.wait_ge(dve_emptied, basee + (emptied(b) - 1))
                for tok in range(TOK):
                    v = x_sb[:, tok, COLS * j:COLS * (j + 1)]
                    last = dve.tensor_tensor(v, bank[2 * (b % 2) + tok][:], v, ALU.add)
                last.then_inc(dve_emptied, 1)

            def square(count, base=0):
                dve.wait_ge(act_emptied, base + count)
                dve.tensor_tensor(stage[:], stage[:], stage[:], ALU.mult).then_inc(sq_ready, 1)

            for n in range(first(B_PROJ), first(B_FF + 2 * NBD)):
                split(n)
                for j in range(NBD):
                    for branch in range(3):
                        b = B_PROJ + 3 * j + branch
                        if n != taken_at(b):
                            continue
                        dve.wait_ge(piece_used, end(b) + 1)
                        dve.wait_ge(act_emptied, emptied(B_PROJ - 1))
                        if branch == 0 and j:
                            dve.wait_ge(tr_made, G_MERGED + 2 * j)
                        for tok in range(TOK):
                            gate = gates[:, tok, D * branch + COLS * j:D * branch + COLS * (j + 1)]
                            src, dst = bank[2 * (b % 2) + tok][:], stage[:, tok, :]
                            if branch == 0:
                                step(dve.tensor_tensor(dst, src, gate, ALU.mult))
                            else:
                                step(dve.tensor_tensor(junk[:, 0:COLS], src, gate, ALU.mult))
                                step(dve.tensor_tensor(dst, dst, junk[:, 0:COLS], ALU.add))
                        dve.sem_inc(dve_emptied, 1)
                        if branch == 2:
                            dve.sem_inc(merged_ready, 1)
                    for a in range(2):
                        if n == merged_end(j) + 6 + a:
                            plain_lo(G_MERGED + 2 * j + a, 4 * j + 2 * a, lhs_a)
                    if n == taken_at(B_WO + j):
                        add_to_x(B_WO + j, j)
                    for a in range(2):
                        if n == end(B_WO + j) + 6 + a:
                            operand_lo(G_X2 + 2 * j + a, lhs_b, 4 * j + 2 * a, R_N2)
                    if n == taken_at(B_FF + j):
                        square(emptied(B_FF + j))
                    for a in range(2):
                        if n == end(B_FF + j) + 6 + a:
                            plain_lo(G_FF + 2 * j + a, 4 * j + 2 * a, act_parts)
                    if n == taken_at(B_FF + NBD + j):
                        add_to_x(B_FF + NBD + j, j)
                e = end(B_WO + NBD - 1)
                if n == e + 4:
                    dve.wait_ge(squares, 4 + TOK * NBD)
                    step(dve.tensor_reduce(ss_two, ss_2.rearrange("p (t n) -> p t n", t=TOK), AX_X,
                                           ALU.add))
                    variance(ss_two, 2, D)
                if n == e + 6:
                    inverse_root(6, 2, r_2, norm2_ready)

            with dve.Fori(0, QUARTERS - 1) as i:
                n0, b0 = first(B_FF + 2 * NBD), B_FF + 2 * NBD
                by_n, by_g, by_b = i * (2 * NBD * PPB), i * (2 * NBD), i * NBD
                for m in range(2 * NBD * PPB):
                    split(n0 + m, base=by_n)
                    if m == 2:
                        add_to_x(b0 - 1, NBD - 1, base=by_n, basee=by_b)
                    for k in range(NBD):
                        if m == PPB * k + 10:
                            square(emptied(b0 + k), base=by_b)
                        for a in range(2):
                            if m == PPB * k + 13 + a:
                                plain_lo(G_FF + 2 * NBD + 2 * k + a, 4 * k + 2 * a, act_parts,
                                          base=by_g)
                        if m == PPB * (NBD + k) + 10:
                            add_to_x(b0 + NBD + k, k, base=by_n, basee=by_b)
            dve.wait_ge(piece_used, end(B_END - 1) + 1)
            dve.wait_ge(dve_emptied, emptied(B_END - 1) - 1)
            for tok in range(TOK):
                v = x_sb[:, tok, D - COLS:D]
                dve.tensor_tensor(v, bank[2 * ((B_END - 1) % 2) + tok][:], v,
                                  ALU.add).then_inc(tail_ready, 1)

        @block.tensor
        def _(pe):
            def products(n, b, k, lhs, tiles, base=0):
                pe.wait_ge(lo_ready, base + (n + 1))
                hi, lo = whi[n % RING], wlo[n % RING]
                for kk in range(PK):
                    for tok in range(TOK):
                        s = slice(P * tok, P * (tok + 1))
                        dst = bank[2 * (b % 2) + tok][:]
                        for i, (part, w) in enumerate(((1, hi), (0, hi), (0, lo))):
                            last = pe.matmul(dst, lhs[:, part, k + kk, s], w[:, kk, :],
                                             start=(k + kk == 0 and i == 0),
                                             stop=(k + kk == tiles - 1 and i == 2))
                last.then_inc(piece_used, 1)

            def bank_free(b, base_a=0, base_d=0):
                if b < 2:
                    return
                if by_dve(b - 2):
                    pe.wait_ge(dve_emptied, base_d + emptied(b - 2))
                else:
                    pe.wait_ge(act_emptied, base_a + emptied(b - 2))

            def transposes(g, sources, base=0):
                for i, src in enumerate(sources):
                    last = pe.transpose(bank[tr_bank(g)][:, P * i:P * (i + 1)], src, ident[:])
                last.then_inc(tr_made, 1)

            def token_tiles(src, k):
                return [src[:, tok, P * (k + j):P * (k + j + 1)] for j in range(PK) for tok in range(TOK)]

            def head_tiles(region, at):
                return [region[:, 512 * at + P * i:512 * at + P * (i + 1)] for i in range(4)]

            def fp32_sum(dst, pairs):
                for i, (a, b) in enumerate(pairs):
                    last = pe.matmul(dst, a, b, start=(i == 0), stop=(i == len(pairs) - 1))
                return last

            def memory_scores(h):
                for tok in range(TOK):
                    last = fp32_sum(scores[:, 256 * tok:256 * (tok + 1)],
                                    [(mq_sb[:, 512 * h + 256 * c + P * tok:512 * h + 256 * c + P * (tok + 1)],
                                      mk_sb[:, 512 * h + 256 * c:512 * h + 256 * (c + 1)])
                                     for c in range(2)])
                last.then_inc(scores_made, 1)

            def fox_scores(h):
                q = q_sb[:, 256 * h:256 * (h + 1)]
                k = k_sb[:, 256 * h:256 * (h + 1)]
                nlf_t = [[nlf_wide[:, h % 2, tok, part, :] for part in (1, 0)] for tok in range(TOK)]
                pe.wait_ge(nlf_spread, h + 1)
                pe.wait_ge(upto_ready, 1)
                dst = scores[:, 0:P]
                pe.matmul(dst, q[:, 0:P], k[:, 0:P], start=True, stop=False)
                for part in nlf_t[0]:
                    pe.matmul(dst, part, upto[:, 0:P], start=False, stop=False)
                pe.matmul(dst, ident_h[:], mask[:], start=False, stop=True)
                dst, own = scores[:, P:3 * P], scores[:, 2 * P:3 * P]
                pe.matmul(dst, q[:, P:2 * P], k, start=True, stop=False)
                for part in nlf_t[0]:
                    pe.matmul(dst, part, upto[:], start=False, stop=False)
                for part in nlf_t[1]:
                    pe.matmul(own, part, upto[:, 0:P], start=False, stop=False)
                pe.matmul(own, ident_h[:], mask[:], start=False, stop=True).then_inc(scores_made, 1)

            pe.wait_ge(consts, 4)
            for _ in range(WARM):
                pe.matmul(bank[7][:, 0:P], ident_h[:], ident_h[:], start=True, stop=True)

            for m in range(first(B_GATE + STRAIGHT)):
                b = block_of(m)
                if m < PPB:
                    pe.wait_ge(op_ready, m + 1)
                for j in range(4):
                    for slot, gap, g, region, count in ((MK_SLOT, 2, G_MK, mk_sb, 1),
                                                        (MQ_SLOT, 1, G_MQ, mq_sb, 2),
                                                        (FQ_SLOT, 1, G_FQ, q_sb, 3),
                                                        (FK_SLOT, 1, G_FK, k_sb, 4)):
                        if m == slot + gap * j:
                            pe.wait_ge(normed, count)
                            if g + j:
                                pe.wait_ge(tr_taken, g + j)
                            transposes(g + j, head_tiles(region, j))
                if m == F_SLOT:
                    pe.wait_ge(op_ready, 2 * PPB)
                    pe.wait_ge(wf_lo, 1)
                    for kk in range(KT):
                        for part in (1, 0):
                            last = pe.matmul(o_bank[:, 0:TOK * P],
                                             wf_parts[:, WF_WIDE * kk:WF_WIDE * kk + P],
                                             lhs_a[:, part, kk, :], start=(kk == 0 and part == 1),
                                             stop=(kk == KT - 1 and part == 0))
                    last.then_inc(f_made, 1)
                if m == F_SLOT + 4:
                    pe.wait_ge(f_rows_ready, 1)
                    for tok in range(TOK):
                        last = pe.matmul(o_bank[:, 256 + FH * tok:256 + FH * (tok + 1)],
                                         f_rows[0:WF_WIDE, P * tok:P * (tok + 1)],
                                         f_sum[0:WF_WIDE, :], start=True, stop=True)
                    last.then_inc(f_summed, 1)
                for k in range(MH + FH):
                    s = head_slot(k)
                    if m == s:
                        if k:
                            pe.wait_ge(exp_done, 2 * k)
                        pe.wait_ge(tr_taken, (G_MQ + k if k < MH else G_FK + (k - MH) // 2) + 1)
                        if k < MH:
                            memory_scores(k)
                        else:
                            fox_scores(k - MH)
                    if m == s + 4:
                        pe.wait_ge(p_normed, k + 1)
                        if k < MH:
                            parts = [prob[:, 256 * tok + P * kt:256 * tok + P * (kt + 1)]
                                     for kt in range(2) for tok in range(TOK)]
                        else:
                            parts = [prob[:, 0:P], prob[:, P:2 * P], prob[:, 2 * P:3 * P]]
                        for i, src in enumerate(parts):
                            last = pe.transpose(p_bank[:, P * i:P * (i + 1)], src, ident[:])
                        last.then_inc(pt_made, 1)
                    if m == s + 6:
                        pe.wait_ge(pt_taken, k + 1)
                        if k:
                            pe.wait_ge(pv_taken, k)
                        if k == 0:
                            pe.wait_ge(act_emptied, emptied(B_MQ - 1))
                        if k < MH:
                            for c in range(2):
                                v = slice(256 * k + P * c, 256 * k + P * (c + 1))
                                last = fp32_sum(o_bank[:, 256 * c:256 * (c + 1)],
                                                [(mv_sb[:, kt, v], prob_t[:, 256 * kt:256 * (kt + 1)])
                                                 for kt in range(TOK)])
                        else:
                            h = k - MH
                            v = slice(P * h, P * (h + 1))
                            pe.wait_ge(act_emptied, emptied(B_FV + h // 4))
                            pe.matmul(o_bank[:, 0:256], v_sb[:, 0, v], prob_t[:, 0:256],
                                      start=True, stop=False)
                            last = pe.matmul(o_bank[:, P:256], v_sb[:, 1, v], prob_t[:, 256:384],
                                             start=False, stop=True)
                        last.then_inc(pv_made, 1)
                for c in range(CW // P):
                    if m == CONV_SLOT + 3 * c:
                        pe.wait_ge(dve_emptied, 2)
                        pe.wait_ge(act_emptied, emptied(B_CB + c // 4))
                        pe.wait_ge(tr_taken, max(G_CONV, G_CONV + c - 3))
                        if c == 2:
                            pe.wait_ge(pv_taken, MH + FH)
                        transposes(G_CONV + c, [v[:, 256 * c + P * tok:256 * c + P * (tok + 1)]
                                                for v in (conv_u, conv_b) for tok in range(TOK)])
                if m == first(b):
                    bank_free(b)
                products(m, b, PK * (m - first(b)), lhs_b if b < B_MQ else lhs_a, KT)

            with pe.Fori(0, (B_PROJ - B_GATE - STRAIGHT) // 2) as i:
                for j in range(2 * PPB):
                    m = first(B_GATE + STRAIGHT) + j
                    b, k = block_of(m), j % PPB
                    if k == 0:
                        bank_free(b, base_a=i * 2)
                    products(m, b, PK * k, lhs_a, KT, base=i * (2 * PPB))

            for m in range(first(B_PROJ), first(B_FF + 2 * NBD)):
                b = block_of(m)
                for j in range(NBD):
                    for e, ready, count, g, src, k0 in (
                            (merged_end(j), merged_ready, j + 1, G_MERGED, stage, 0),
                            (end(B_WO + j), dve_emptied, emptied(B_WO + j), G_X2, x_sb, NBD * j),
                            (end(B_FF + j), sq_ready, j + 1, G_FF, stage, 0)):
                        for a in range(2):
                            if m == e + 3 + a:
                                pe.wait_ge(ready, count)
                                pe.wait_ge(tr_taken, g + 2 * j + a - 3)
                                transposes(g + 2 * j + a, token_tiles(src, k0 + PK * a))
                if m == first(b):
                    bank_free(b)
                if b < B_WO:
                    branch = (b - B_PROJ) % 3
                    if m == first(B_PROJ):
                        pe.wait_ge(y_lo, CW // P)
                        pe.wait_ge(pv_taken, MH + FH)
                    lhs, at = ((y_parts, 0), (lhs_b, 0), (lhs_b, CW // P))[branch]
                    products(m, b, PK * (m - first(b)), lhs[:, :, at:at + CW // P, :], CW // P)
                    continue
                piece = m - first(b)
                if b == B_WO:
                    pe.wait_ge(tr_taken, G_MERGED + piece + 1)
                if b == B_FF:
                    pe.wait_ge(tr_taken, G_X2 + piece + 1)
                if b == B_FF + NBD:
                    pe.wait_ge(tr_taken, G_FF + piece + 1)
                lhs = lhs_a if b < B_FF else lhs_b if b < B_FF + NBD else act_parts
                products(m, b, PK * piece, lhs, KT)

            with pe.Fori(0, QUARTERS - 1) as i:
                n0, b0, g0 = first(B_FF + 2 * NBD), B_FF + 2 * NBD, G_FF + 2 * NBD
                by_n, by_g, by_b = i * (2 * NBD * PPB), i * (2 * NBD), i * NBD
                for m in range(2 * NBD * PPB):
                    b, k = divmod(m, PPB)
                    for j in range(NBD):
                        for a in range(2):
                            if m == PPB * j + 10 + a:
                                pe.wait_ge(sq_ready, by_b + (NBD + j + 1))
                                pe.wait_ge(tr_taken, by_g + (g0 + 2 * j + a - 3))
                                transposes(g0 + 2 * j + a, token_tiles(stage, PK * a))
                    if k == 0:
                        bank_free(b0 + b, base_a=by_b, base_d=by_b)
                    if b == NBD:
                        pe.wait_ge(tr_taken, by_g + (g0 + k + 1))
                    products(n0 + m, b0 + b, PK * k, lhs_b if b < NBD else act_parts, KT, base=by_n)


_INS = ["x", "mem", "x_t", "mem_t", "cols", "w_in", "w_mem_kv", "w_conv_out", "w_fox_out",
        "w_mem_out", "w_out", "w_up", "w_down"]


def tiles(a):
    return a.reshape(-1, P, a.shape[-1]).transpose(1, 0, 2).reshape(P, -1)


def kernel(**inputs):
    import numpy as np
    import concourse.bacc as bacc
    from concourse.bass_utils import run_bass_kernel_spmd as run

    inputs = dict(inputs)
    for name in ("x", "mem"):
        inputs[name + "_t"] = tiles(np.asarray(inputs[name])[0].T)
    gains = [np.asarray(inputs[n]).reshape(-1, P).T
             for n in ("norm1_g", "mem_norm_g", "norm2_g", "conv_w", "fox_q_g", "fox_k_g",
                       "mem_q_g", "mem_k_g")]
    inputs["cols"] = np.concatenate(
        gains + [tiles(np.asarray(inputs["w_in"])[:, C_F:C_F + FH]),
                 np.broadcast_to(np.asarray(inputs["b_f"]), (P, FH))], axis=1)

    nc = bacc.Bacc("TRN2", target_bir_lowering=False, num_devices=1)
    arrays, aps = {}, {}
    for name in _INS:
        a = np.ascontiguousarray(inputs[name])
        arrays[f"in_{name}"] = a
        aps[name] = nc.dram_tensor(f"in_{name}", a.shape, mybir.dt.from_np(a.dtype),
                                   kind="ExternalInput").ap()
    out = nc.dram_tensor("out", inputs["x"].shape, F32, kind="ExternalOutput").ap()
    build(nc, aps, out)
    return run(nc, [arrays], core_ids=[0]).results[0]["out"]
```
